# Optimizing a Trainium2 kernel written in Bass

```python
import math
import jax, jax.numpy as jnp
from jax import lax
import numpy as np

D_MODEL = 1024
BATCH = 1
SEQ = 256
DEPTH = 1
DEC_BATCH = 1
DEC_SEQ = 1024
PAST_LEN = 128

GRID_W = 64
RW_HEAD = 64
RW_HEADS = D_MODEL // RW_HEAD
RW_WIDTH = RW_HEADS * RW_HEAD
W_RANK = 64
A_RANK = 64
G_RANK = 128
DECAY_SCALE = math.exp(-0.5)
GN_EPS = 64e-5
ATT_HEAD = 128
ATT_Q_HEADS = D_MODEL // ATT_HEAD
ATT_KV_HEADS = 2
ATT_GROUP = ATT_Q_HEADS // ATT_KV_HEADS
ATT_Q = ATT_Q_HEADS * ATT_HEAD
ATT_KV = ATT_KV_HEADS * ATT_HEAD
Q_BLOCK = 128
ROPE_THETA = 10000.0
RMS_EPS = 1e-6
N_BRANCH = 2
D_FF = 4 * D_MODEL
LN_EPS = 1e-5
ALPHA = (2 * DEPTH) ** 0.25
BETA = (8 * DEPTH) ** -0.25
RW_SPLIT = [RW_WIDTH, RW_WIDTH, RW_WIDTH, 2 * W_RANK, 2 * A_RANK, G_RANK]
RW_COLS = sum(RW_SPLIT)
IN_SPLIT = [RW_COLS, ATT_Q, ATT_KV, ATT_KV, N_BRANCH * D_MODEL]
IN_COLS = sum(IN_SPLIT)

kernel_name = 'hybrid_rwkv7_axial_gqa_encoder'

def _offsets(sizes):
    out, acc = [], 0
    for s in sizes[:-1]:
        acc += s
        out.append(acc)
    return out

def _layernorm(x, g, b, eps):
    xf = x.astype(jnp.float32)
    mu = jnp.mean(xf, axis=-1, keepdims=True)
    var = jnp.mean(jnp.square(xf - mu), axis=-1, keepdims=True)
    return ((xf - mu) * lax.rsqrt(var + eps) * g + b).astype(x.dtype)

def _rmsnorm(x, g):
    xf = x.astype(jnp.float32)
    return (xf * lax.rsqrt(jnp.mean(xf * xf, axis=-1, keepdims=True) + RMS_EPS) * g).astype(x.dtype)

def _wkv_scan(r, w, kh, ak, v, kt, reverse):
    T, B, H, N = r.shape
    def step(S, inp):
        r_t, w_t, kh_t, ak_t, v_t, kt_t = inp
        sk = jnp.einsum('bhvk,bhk->bhv', S, kh_t)
        S = S * w_t[:, :, None, :] - sk[..., None] * ak_t[:, :, None, :] + v_t[..., None] * kt_t[:, :, None, :]
        return S, jnp.einsum('bhvk,bhk->bhv', S, r_t)
    S0 = jnp.zeros((B, H, N, N), jnp.float32)
    _, o = lax.scan(step, S0, (r, w, kh, ak, v, kt), reverse=reverse)
    return o

def _rwkv7_branch(z, mu_prev, mu_next, w0, w_up, a0, a_up, g_up, k_k, k_a, r_k, gn_g, gn_b):
    B, T, _ = z.shape
    H, N, C = RW_HEADS, RW_HEAD, RW_WIDTH
    f32 = jnp.float32
    z_prev = jnp.pad(z[:, :-1], ((0, 0), (1, 0), (0, 0)))
    z_next = jnp.pad(z[:, 1:], ((0, 0), (0, 1), (0, 0)))
    z = z + mu_prev * (z_prev - z) + mu_next * (z_next - z)
    r, k, v, wd, ad, gd = jnp.split(z, _offsets(RW_SPLIT), axis=-1)
    w_log = w0 + jnp.einsum('btdr,drc->btdc', jnp.tanh(wd.reshape(B, T, 2, W_RANK)), w_up)
    decay = jnp.exp(-DECAY_SCALE * jax.nn.sigmoid(w_log.astype(f32)))
    a = jax.nn.sigmoid((a0 + jnp.einsum('btdr,drc->btdc', ad.reshape(B, T, 2, A_RANK), a_up)).astype(f32))
    g = jnp.einsum('btr,rc->btc', jax.nn.sigmoid(gd), g_up)
    kf = k.astype(f32)
    kappa = (kf * k_k).reshape(B, T, 1, H, N)
    kappa_hat = kappa / jnp.maximum(jnp.sqrt(jnp.sum(kappa * kappa, axis=-1, keepdims=True)), 1e-12)
    k_tilde = (kf[:, :, None, :] * (1.0 + (a - 1.0) * k_a)).reshape(B, T, 2, H, N)
    ak = a.reshape(B, T, 2, H, N) * kappa_hat
    decay = decay.reshape(B, T, 2, H, N)
    r_h = r.astype(f32).reshape(B, T, H, N)
    v_h = v.astype(f32).reshape(B, T, H, N)
    tm = lambda u: jnp.moveaxis(u, 1, 0)
    r_t, v_t, kh_t = tm(r_h), tm(v_h), tm(kappa_hat[:, :, 0])
    o_f = _wkv_scan(r_t, tm(decay[:, :, 0]), kh_t, tm(ak[:, :, 0]), v_t, tm(k_tilde[:, :, 0]), False)
    o_b = _wkv_scan(r_t, tm(decay[:, :, 1]), kh_t, tm(ak[:, :, 1]), v_t, tm(k_tilde[:, :, 1]), True)
    o = jnp.moveaxis(o_f + o_b, 0, 1)
    o = _layernorm(o, gn_g.reshape(H, N), gn_b.reshape(H, N), GN_EPS)
    bonus = jnp.sum(r_h * jnp.sum(k_tilde, axis=2) * r_k.reshape(H, N), axis=-1, keepdims=True) * v_h
    return ((o + bonus).reshape(B, T, C) * g).astype(z.dtype)

def _axial_rope(T):
    rows = T // GRID_W
    row = jnp.repeat(jnp.arange(rows, dtype=jnp.float32), GRID_W)
    col = jnp.tile(jnp.arange(GRID_W, dtype=jnp.float32), rows)
    half = ATT_HEAD // 2
    inv = ROPE_THETA ** (-jnp.arange(0, half, 2, dtype=jnp.float32) / half)
    ang = jnp.stack([row[:, None] * inv, col[:, None] * inv], axis=1)
    ang = jnp.broadcast_to(ang[:, :, None, :], (T, 2, 2, half // 2)).reshape(T, ATT_HEAD)
    return jnp.cos(ang), jnp.sin(ang)

def _apply_rope(x, cos, sin):
    xs = x.reshape(x.shape[:-1] + (2, 2, ATT_HEAD // 4))
    rot = jnp.stack([-xs[..., 1, :], xs[..., 0, :]], axis=-2).reshape(x.shape)
    return (x * cos[None, :, None, :] + rot * sin[None, :, None, :]).astype(x.dtype)

def _attention_branch(q, k, v, q_norm, k_norm):
    B, T, _ = q.shape
    q = _rmsnorm(q.reshape(B, T, ATT_Q_HEADS, ATT_HEAD), q_norm)
    k = _rmsnorm(k.reshape(B, T, ATT_KV_HEADS, ATT_HEAD), k_norm)
    v = v.reshape(B, T, ATT_KV_HEADS, ATT_HEAD)
    cos, sin = _axial_rope(T)
    q = _apply_rope(q, cos, sin)
    k = _apply_rope(k, cos, sin)
    qb = q.reshape(B, T // Q_BLOCK, Q_BLOCK, ATT_KV_HEADS, ATT_GROUP, ATT_HEAD)
    qb = jnp.moveaxis(qb, 1, 0)
    scale = ATT_HEAD ** -0.5
    def block(qi):
        s = jnp.einsum('bqhgd,bkhd->bhgqk', qi, k).astype(jnp.float32) * scale
        p = jax.nn.softmax(s, axis=-1).astype(v.dtype)
        return jnp.einsum('bhgqk,bkhd->bqhgd', p, v)
    o = lax.map(block, qb)
    return jnp.moveaxis(o, 0, 1).reshape(B, T, ATT_Q)

def _encoder_layer(x, w_in, rw_mu_prev, rw_mu_next, rw_w0, rw_w_up, rw_a0, rw_a_up, rw_g_up,
                   rw_k_k, rw_k_a, rw_r_k, rw_gn_g, rw_gn_b, q_norm, k_norm,
                   w_proj_rwkv, w_proj_attn, w_out, ln1_g, ln1_b, w_ff1, w_ff2, ln2_g, ln2_b):
    B, T, D = x.shape
    z = jnp.einsum('btd,dc->btc', x, w_in)
    z_rw, q, k, v, gate_logits = jnp.split(z, _offsets(IN_SPLIT), axis=-1)
    o_rw = _rwkv7_branch(z_rw, rw_mu_prev, rw_mu_next, rw_w0, rw_w_up, rw_a0, rw_a_up, rw_g_up,
                         rw_k_k, rw_k_a, rw_r_k, rw_gn_g, rw_gn_b)
    o_att = _attention_branch(q, k, v, q_norm, k_norm)
    gates = jax.nn.sigmoid(gate_logits.astype(jnp.float32)).astype(x.dtype).reshape(B, T, N_BRANCH, D)
    merged = (gates[:, :, 0] * jnp.einsum('btc,cd->btd', o_rw, w_proj_rwkv)
              + gates[:, :, 1] * jnp.einsum('btc,cd->btd', o_att, w_proj_attn))
    mix = jnp.einsum('btd,de->bte', merged, w_out)
    h = _layernorm(ALPHA * x + mix, ln1_g, ln1_b, LN_EPS)
    ff = jnp.einsum('btf,fd->btd', jnp.square(jax.nn.relu(jnp.einsum('btd,df->btf', h, w_ff1))), w_ff2)
    return _layernorm(ALPHA * h + ff, ln2_g, ln2_b, LN_EPS)

def _trunk(x, params):
    h = x
    for l in range(DEPTH):
        h = _encoder_layer(h, *[p[l] for p in params])
    return h

def setup_inputs(seed: int = 0) -> dict:
    key = jax.random.key(seed)
    ks = iter(jax.random.split(key, 40))
    f32 = jnp.float32
    def nrm(shape, scale):
        return jax.random.normal(next(ks), shape, f32) * scale
    def unif(shape, lo, hi):
        return jax.random.uniform(next(ks), shape, f32, lo, hi)
    L, C, D = DEPTH, RW_WIDTH, D_MODEL
    return {
        'x_prompt': nrm((BATCH, SEQ, D), 1.0),
        'x_sample': nrm((DEC_BATCH, DEC_SEQ, D), 1.0),
        'w_in': nrm((L, D, IN_COLS), D ** -0.5),
        'rw_mu_prev': unif((L, RW_COLS), 0.0, 0.5),
        'rw_mu_next': unif((L, RW_COLS), 0.0, 0.5),
        'rw_w0': nrm((L, 2, C), 0.5) - 1.0,
        'rw_w_up': nrm((L, 2, W_RANK, C), 0.5 * W_RANK ** -0.5),
        'rw_a0': nrm((L, 2, C), 0.5),
        'rw_a_up': nrm((L, 2, A_RANK, C), 0.5 * A_RANK ** -0.5),
        'rw_g_up': nrm((L, G_RANK, C), G_RANK ** -0.5),
        'rw_k_k': 0.85 + nrm((L, C), 0.1),
        'rw_k_a': 1.0 + nrm((L, C), 0.1),
        'rw_r_k': nrm((L, C), 0.1),
        'rw_gn_g': 1.0 + nrm((L, C), 0.1),
        'rw_gn_b': nrm((L, C), 0.01),
        'q_norm': 1.0 + nrm((L, ATT_HEAD), 0.1),
        'k_norm': 1.0 + nrm((L, ATT_HEAD), 0.1),
        'w_proj_rwkv': nrm((L, C, D), BETA * C ** -0.5),
        'w_proj_attn': nrm((L, ATT_Q, D), BETA * ATT_Q ** -0.5),
        'w_out': nrm((L, D, D), BETA * D ** -0.5),
        'ln1_g': 1.0 + nrm((L, D), 0.1),
        'ln1_b': nrm((L, D), 0.01),
        'w_ff1': nrm((L, D, D_FF), BETA * D ** -0.5),
        'w_ff2': nrm((L, D_FF, D), BETA * D_FF ** -0.5),
        'ln2_g': 1.0 + nrm((L, D), 0.1),
        'ln2_b': nrm((L, D), 0.01),
    }

def reference(x_prompt, x_sample, w_in, rw_mu_prev, rw_mu_next, rw_w0, rw_w_up, rw_a0, rw_a_up,
              rw_g_up, rw_k_k, rw_k_a, rw_r_k, rw_gn_g, rw_gn_b, q_norm, k_norm,
              w_proj_rwkv, w_proj_attn, w_out, ln1_g, ln1_b, w_ff1, w_ff2, ln2_g, ln2_b):
    params = (w_in, rw_mu_prev, rw_mu_next, rw_w0, rw_w_up, rw_a0, rw_a_up, rw_g_up,
              rw_k_k, rw_k_a, rw_r_k, rw_gn_g, rw_gn_b, q_norm, k_norm,
              w_proj_rwkv, w_proj_attn, w_out, ln1_g, ln1_b, w_ff1, w_ff2, ln2_g, ln2_b)
    y_prompt = _trunk(x_prompt, params)
    y_sample = _trunk(x_sample, params)
    return (y_prompt, y_sample)


_drawn_inputs = setup_inputs


def setup_inputs(seed=0):
    import zlib

    import numpy as np

    out = dict(_drawn_inputs(seed))
    spreads = {}
    factors = {'rw_w0': 2.805,
     'rw_w_up': 8.0,
     'rw_a0': 2.978,
     'rw_a_up': 4.452,
     'rw_k_k': 22.137,
     'rw_k_a': 4.955,
     'rw_gn_g': 6.171,
     'rw_gn_b': 64.0,
     'q_norm': 8.0,
     'k_norm': 8.0,
     'w_proj_attn': 3.366,
     'ln1_b': 5.453,
     'ln2_b': 5.646}
    for name, (base, spread) in spreads.items():
        noise = np.random.default_rng([zlib.crc32(name.encode()), seed]).standard_normal(out[name].shape)
        drawn = base * np.exp(spread * noise) if base else spread * noise
        out[name] = __import__('jax').numpy.asarray(drawn.astype(out[name].dtype))
    for name, factor in factors.items():
        out[name] = (out[name] * factor).astype(out[name].dtype)
    return out
```

```python
import math
from contextlib import ExitStack

import concourse.bass as bass
from concourse import mybir

F32 = mybir.dt.float32
ALU = mybir.AluOpType
ACT = mybir.ActivationFunctionType
AX = mybir.AxisListType

D = 1024
KT = D // 128
SEQ_S, SEQ_P = 1024, 256
T = SEQ_S + SEQ_P
SPANS = [(0, 512), (512, 512), (1024, 256)]
PAIRS = 8
CH = 64
GRP = 4
GT = CH * GRP
STEPS = T // GT
NCH = T // CH
DECAY_SCALE = math.exp(-0.5)
GN_EPS, RMS_EPS, LN_EPS = 64e-5, 1e-6, 1e-5
ALPHA = 2 ** 0.25
QH, KVH, HD = 8, 2, 128
ATT_SCALE = HD ** -0.5
FFG = 4
B_R, B_K, B_V, B_LOW, B_Q, B_AK, B_AV, B_GATE = 0, 8, 16, 24, 27, 35, 37, 39
C_ID, C_PERM, C_ONES, C_BONES = 0, 128, 256, 384
C_MAB, C_MAK = 512, 768
C_LVL = 1024
C_ID32 = C_LVL + 320
C_BLK = C_ID32 + 32
C_SEL = C_BLK + 64
C_FLAG = C_SEL + 2
C_EPS = C_FLAG + 2 * STEPS
C_ID64 = C_EPS + 4
NCONST = C_ID64 + 64
(P_MP, P_MN, P_W0, P_A0, P_KK, P_KA, P_RK, P_GG, P_GB) = (0, 3, 6, 8, 10, 11, 12, 13, 14)
P_OM, P_OKA, P_OKA2 = 15, 18, 19
NPAIR = 15
G_MP, G_MN, G_QK, G_L1G, G_L1B, G_L2G, G_L2B = 0, 3, 6, 16, 24, 32, 40
NGLOB = 48
G_OM = 48


def dense_block(pe, ps, bank, w, act):
    for j, (t0, n) in enumerate(SPANS):
        for k in range(KT):
            last = pe.matmul(ps[:, bank + j, 0:n], w[:, 128 * k:128 * k + 128], act[:, k, t0:t0 + n],
                             start=(k == 0), stop=(k == KT - 1))
    return last


def settle(eng, passed):
    eng.sem_inc(passed, 1)


def wide(pe, ps, bank, lhsT, src):
    for j, (t0, n) in enumerate(SPANS):
        last = pe.matmul(ps[:, bank + j, 0:n], lhsT, src[:, t0:t0 + n], start=True, stop=True)
    return last


class Chain:

    def __init__(self, eng, sem, base=0):
        self.eng, self.sem, self.base, self.n = eng, sem, base, 0

    def __call__(self, ins):
        self.n += 1
        ins.then_inc(self.sem, 1)

    def sync(self):
        self.eng.wait_ge(self.sem, self.base + self.n)

    def then(self, ins):
        self(ins)
        self.sync()


class Stage:

    def __init__(self, nc, tag):
        self.nc, self.tag, self.ctx, self.used = nc, tag, ExitStack(), []

    def __enter__(self):
        self.ctx.__enter__()
        return self

    def __exit__(self, *a):
        self.ctx.__exit__(*a)
        self.nc.clear_and_free_semaphores(self.used)
        self.nc.all_engine_barrier()

    def sb(self, name, *shape):
        return self.ctx.enter_context(self.nc.sbuf_tensor(f"{self.tag}_{name}", list(shape), F32))

    def psum(self):
        return self.ctx.enter_context(self.nc.psum_tensor(f"{self.tag}_ps", [128, 8, 512], F32))

    def sem(self, name):
        self.used.append(self.nc.alloc_semaphore(f"{self.tag}_{name}"))
        return self.used[-1]

    def sems(self, names):
        return [self.sem(n) for n in names.split()]

    def block(self):
        return self.ctx.enter_context(self.nc.Block())


def set_of(ps, bank):
    return ps[:, bank:bank + 3, :].rearrange("p b n -> p (b n)")[:, 0:T]


def load_stage(nc, hbm, xT, cst, glob):
    with Stage(nc, "ld") as st:
        loaded, = st.sems("loaded")
        om, = st.sems("om")
        block = st.block()

        @block.sync
        def _(sp):
            sp.dma_start(cst[:, :], hbm["consts"]).then_inc(loaded, 16)
            sp.dma_start(glob[:, 0:NGLOB], hbm["glob"]).then_inc(loaded, 16)
            sp.dma_start(xT[:, :, :], hbm["xT"].rearrange("(k p) t -> p k t", p=128)).then_inc(loaded, 16)
            sp.wait_ge(loaded, 48)

        @block.vector
        def _(dve):
            ch = Chain(dve, om)
            dve.wait_ge(loaded, 48)
            ch.then(dve.tensor_tensor(glob[:, G_OM:G_OM + 3], glob[:, G_MP:G_MP + 3], glob[:, G_MN:G_MN + 3], ALU.add))
            ch.then(dve.tensor_scalar(glob[:, G_OM:G_OM + 3], glob[:, G_OM:G_OM + 3], -1.0, 1.0, ALU.mult, ALU.add))


def attention_heads(nc, hbm, xT, cst, glob, qs, qp, ks, kp, vt):
    with Stage(nc, "qk") as st:
        w = [st.sb(f"w{i}", 128, D) for i in range(2)]
        wv = st.sb("wv", 128, 2, D)
        cos, sin = st.sb("cos", 128, T), st.sb("sin", 128, T)
        sq, zq, rt, xc, tmp = ([st.sb(f"{n}{i}", 128, T) for i in range(2)] for n in ("sq", "zq", "rt", "xc", "tmp"))
        ps = st.psum()
        w_ready = st.sems("w_ready0 w_ready1")
        tab_ready, wv_ready = st.sems("tab_ready wv_ready")
        z_ready, sq_ready, zq_done, stat_ready, rt_ready, zn_ready, rot_ready, xc_ready = st.sems(
            "z_ready sq_ready zq_done stat_ready rt_ready zn_ready rot_ready xc_ready")
        rot_used, rope_done, v_ready, v_used, ln_done, passed = st.sems("rot_used rope_done v_ready v_used ln_done passed")
        ones, perm = cst[:, C_ONES:C_ONES + 128], cst[:, C_PERM:C_PERM + 128]
        nh = QH + KVH
        block = st.block()

        @block.sync
        def _(sp):
            for sem in (rot_used, rope_done):
                sp.sem_inc(sem, 1)
            def load(s, head):
                sp.dma_start(w[s][:, :], hbm["w_in"][B_Q + head:B_Q + head + 1, :, :].rearrange("a p n -> (a p) n")
                             if isinstance(head, int) else
                             hbm["w_in"][bass.ds(head + B_Q, 1), :, :].rearrange("a p n -> (a p) n")).then_inc(w_ready[s], 16)

            load(0, 0)
            load(1, 1)
            sp.dma_start(cos[:, :], hbm["cos"]).then_inc(tab_ready, 16)
            sp.dma_start(sin[:, :], hbm["sin"]).then_inc(tab_ready, 16)
            sp.dma_start(wv[:, :, :], hbm["w_in"][B_AV:B_AV + 2, :, :].rearrange("a p n -> p a n")).then_inc(wv_ready, 16)
            with sp.Fori(1, nh // 2, 1) as i:
                for s in range(2):
                    sp.wait_ge(z_ready, i * 2 + (s - 1))
                    load(s, i * 2 + s)
            sp.wait_ge(tab_ready, 32)

        @block.tensor
        def _(pe):
            with pe.Fori(0, nh // 2, 1) as i:
                for s in range(2):
                    pe.wait_ge(w_ready[s], i * 16 + 16)
                    pe.wait_ge(rot_used, i * 2 + 1)
                    dense_block(pe, ps, 3 * s, w[s], xT).then_inc(z_ready, 1)
                for s in range(2):
                    pe.wait_ge(sq_ready, i * 2 + s + 1)
                    pe.wait_ge(zq_done, i * 2 + s + 1)
                    wide(pe, ps, 3 * s, ones, sq[s]).then_inc(stat_ready, 1)
                for s in range(2):
                    pe.wait_ge(zn_ready, i * 2 + s + 1)
                    wide(pe, ps, 3 * s, perm, zq[s]).then_inc(rot_ready, 1)
            pe.wait_ge(wv_ready, 16)
            for t in range(T // 128):
                if t >= 2:
                    pe.wait_ge(v_used, t - 1)
                for k in range(KT):
                    last = pe.matmul(ps[:, 6 + t % 2, 0:256], xT[:, k, 128 * t:128 * t + 128],
                                     wv[:, :, 128 * k:128 * k + 128], start=(k == 0), stop=(k == KT - 1))
                last.then_inc(v_ready, 1)

        @block.scalar
        def _(act):
            with act.Fori(0, nh // 2, 1) as i:
                for s in range(2):
                    act.wait_ge(z_ready, i * 2 + s + 1)
                    act.activation(sq[s][:, :], set_of(ps, 3 * s), ACT.Square).then_inc(sq_ready, 1)
                for s in range(2):
                    act.wait_ge(stat_ready, i * 2 + s + 1)
                    act.activation(rt[s][:, :], set_of(ps, 3 * s), ACT.Ln, bias=cst[:, C_EPS:C_EPS + 1],
                                   scale=1.0 / HD).then_inc(ln_done, 1)
                    act.wait_ge(ln_done, i * 2 + s + 1)
                    settle(act, passed)
                    act.activation(rt[s][:, :], rt[s][:, :], ACT.Exp, scale=-0.5).then_inc(rt_ready, 1)
            for t in range(T // 128):
                act.wait_ge(v_ready, t + 1)
                act.activation(vt[:, t, :], ps[:, 6 + t % 2, 0:256], ACT.Copy).then_inc(v_used, 1)

        @block.gpsimd
        def _(pool):
            pool.wait_ge(tab_ready, 32)
            with pool.Fori(0, nh // 2, 1) as i:
                for s in range(2):
                    pool.wait_ge(zn_ready, i * 2 + s + 1)
                    pool.wait_ge(rope_done, i * 4 + 1)
                    pool.tensor_tensor(xc[s][:, :], zq[s][:, :], cos[:, :], ALU.mult).then_inc(xc_ready, 1)

        @block.vector
        def _(dve):
            def heads(i, out_s, out_p, h0):
                n = i * 2 + h0
                for s in range(2):
                    dve.wait_ge(sq_ready, n + s + 1)
                    dve.tensor_scalar(zq[s][:, :], set_of(ps, 3 * s), glob[:, G_QK + (h0 >= QH):G_QK + (h0 >= QH) + 1],
                                      None, ALU.mult).then_inc(zq_done, 1)
                for s in range(2):
                    dve.wait_ge(rt_ready, n + s + 1)
                    dve.tensor_tensor(zq[s][:, :], zq[s][:, :], rt[s][:, :], ALU.mult).then_inc(zn_ready, 1)
                for s in range(2):
                    dve.wait_ge(rot_ready, n + s + 1)
                    dve.wait_ge(tab_ready, 32)
                    dve.tensor_tensor(tmp[s][:, :], set_of(ps, 3 * s), sin[:, :], ALU.mult).then_inc(rot_used, 1)
                    dve.wait_ge(rot_used, n + s + 2)
                    dve.wait_ge(xc_ready, n + s + 1)
                    dve.tensor_tensor(out_s[:, bass.ts(i * 2 + s, SEQ_S)], tmp[s][:, 0:SEQ_S], xc[s][:, 0:SEQ_S],
                                      ALU.add).then_inc(rope_done, 1)
                    dve.tensor_tensor(out_p[:, bass.ts(i * 2 + s, SEQ_P)], tmp[s][:, SEQ_S:T], xc[s][:, SEQ_S:T],
                                      ALU.add).then_inc(rope_done, 1)
                    dve.wait_ge(rope_done, n * 2 + 2 * s + 3)

            with dve.Fori(0, QH // 2, 1) as i:
                heads(i, qs, qp, 0)
            heads(0, ks, kp, QH)


def attention_core(nc, hbm, cst, qs, qp, ks, kp, vt):
    with Stage(nc, "at") as st:
        qt = [st.sb(f"qt{i}", 128, 128) for i in range(2)]
        p = [st.sb(f"p{i}", 128, SEQ_S) for i in range(2)]
        pT = [st.sb(f"pT{i}", 128, SEQ_S) for i in range(2)]
        mx, nm, rs, ri = (st.sb(n, 128, 2) for n in ("mx", "nm", "rs", "ri"))
        ps = st.psum()
        (q_staged, s_ready, nm_ready, exp_done, p_ready, t_ready, pT_dve, pT_act, o_ready, o_done, out_done,
         chain, ri_done) = st.sems("q_staged s_ready nm_ready exp_done p_ready t_ready pT_dve pT_act o_ready o_done out_done chain ri_done")
        ident = cst[:, C_ID:C_ID + 128]
        runs = [(q, k, t0, kv, nk, (QH // KVH) * (nk // 128))
                for q, k, t0, nk in ((qs, ks, 0, SEQ_S), (qp, kp, SEQ_S // 128, SEQ_P)) for kv in range(KVH)]
        block = st.block()

        def schedule(eng, one):
            base = 0
            for run in runs:
                with eng.Fori(0, run[5] // 2, 1) as i:
                    for c in range(2):
                        one(run, i * 2 + c, i * 2 + (base + c), c)
                base += run[5]

        def q_at(run, j):
            return run[0][:, bass.ds(j * 128 + run[3] * run[5] * 128, 128)]

        @block.gpsimd
        def _(pool):
            pool.sem_inc(o_done, 2)
            pool.sem_inc(t_ready, 2)

            def stage(run, j, g, c):
                pool.wait_ge(s_ready, g + 1)
                pool.tensor_copy(qt[c][:, :], q_at(run, j)).then_inc(q_staged, 1)

            schedule(pool, stage)

        @block.tensor
        def _(pe):
            def scores(run, g, c):
                _, k, _, kv, nk, _ = run
                pe.wait_ge(q_staged, g + 1)
                pe.wait_ge(exp_done, g)
                for b in range(0, nk, 512):
                    n = min(512, nk)
                    last = pe.matmul(ps[:, 2 * c + b // 512, 0:n], qt[c][:, :], k[:, kv * nk + b:kv * nk + b + n],
                                     start=True, stop=True)
                last.then_inc(s_ready, 1)

            def transposes(run, g, c):
                nk = run[4]
                pe.wait_ge(p_ready, g + 1)
                pe.wait_ge(pT_dve, g + 1)
                pe.wait_ge(pT_act, g + 1)
                for t in range(nk // 128):
                    last = pe.transpose(ps[:, 4 + t % 2, 128 * (t // 2):128 * (t // 2) + 128], p[c][:, 128 * t:128 * t + 128], ident)
                last.then_inc(t_ready, 1)

            def values(run, g, c):
                _, _, t0, kv, nk, _ = run
                pe.wait_ge(pT_dve, g + 2)
                pe.wait_ge(pT_act, g + 2)
                pe.wait_ge(o_done, g + 1)
                for t in range(nk // 128):
                    at = SEQ_S // 2 * (t % 2) + 128 * (t // 2)
                    last = pe.matmul(ps[:, 6 + c, 0:128], vt[:, t0 + t, 128 * kv:128 * kv + 128], pT[c][:, at:at + 128],
                                     start=(t == 0), stop=(t == nk // 128 - 1))
                last.then_inc(o_ready, 1)

            base = 0
            for run in runs:
                tiles = run[5]
                for c in range(2):
                    scores(run, base + c, c)
                with pe.Fori(0, tiles // 2 - 1, 1) as i:
                    for c in range(2):
                        transposes(run, i * 2 + (base + c), c)
                        scores(run, i * 2 + (base + c + 2), c)
                        values(run, i * 2 + (base + c), c)
                for c in range(2):
                    transposes(run, base + tiles - 2 + c, c)
                    values(run, base + tiles - 2 + c, c)
                base += tiles

        @block.scalar
        def _(act):
            act.sem_inc(exp_done, 1)

            def one(run, j, g, c):
                nk = run[4]
                act.wait_ge(nm_ready, g + 1)
                act.wait_ge(t_ready, g + 1)
                act.activation(p[c][:, 0:nk], ps[:, 2 * c:2 * c + 2, :].rearrange("p b n -> p (b n)")[:, 0:nk], ACT.Exp,
                               bias=nm[:, c:c + 1], scale=ATT_SCALE, accum_out=rs[:, c:c + 1]).then_inc(exp_done, 1)
                act.wait_ge(t_ready, g + 3)
                act.wait_ge(o_ready, g + 1)
                act.activation(pT[c][:, SEQ_S // 2:SEQ_S // 2 + nk // 2], ps[:, 5, 0:nk // 2], ACT.Copy).then_inc(pT_act, 1)

            schedule(act, one)

        @block.vector
        def _(dve):
            def probabilities(run, g, c):
                nk = run[4]
                dve.wait_ge(s_ready, g + 2)
                dve.reduce_max(mx[:, c:c + 1], ps[:, 2 * c:2 * c + 2, :].rearrange("p b n -> p (b n)")[:, 0:nk],
                               AX.X).then_inc(chain, 1)
                dve.wait_ge(chain, g + 1)
                dve.tensor_scalar(nm[:, c:c + 1], mx[:, c:c + 1], -ATT_SCALE, None, ALU.mult).then_inc(nm_ready, 1)
                dve.wait_ge(exp_done, g + 2)
                dve.reciprocal(ri[:, c:c + 1], rs[:, c:c + 1]).then_inc(ri_done, 1)
                dve.wait_ge(ri_done, g + 1)
                dve.tensor_scalar(p[c][:, 0:nk], p[c][:, 0:nk], ri[:, c:c + 1], None, ALU.mult).then_inc(p_ready, 1)

            def transposed(run, g, c):
                nk = run[4]
                dve.wait_ge(t_ready, g + 3)
                dve.tensor_copy(pT[c][:, 0:nk // 2], ps[:, 4, 0:nk // 2]).then_inc(pT_dve, 1)

            def output(run, j, g, c):
                dve.wait_ge(o_ready, g + 2)
                dve.tensor_copy(q_at(run, j), ps[:, 6 + c, 0:128]).then_inc(o_done, 1)

            base = 0
            for run in runs:
                tiles = run[5]
                probabilities(run, base, 0)
                with dve.Fori(0, tiles // 2 - 1, 1) as i:
                    for c in range(2):
                        transposed(run, i * 2 + (base + c), c)
                        probabilities(run, i * 2 + (base + c + 1), 1 - c)
                        output(run, i * 2 + c, i * 2 + (base + c), c)
                transposed(run, base + tiles - 2, 0)
                probabilities(run, base + tiles - 1, 1)
                output(run, tiles - 2, base + tiles - 2, 0)
                transposed(run, base + tiles - 1, 1)
                output(run, tiles - 1, base + tiles - 1, 1)
                base += tiles

        @block.sync
        def _(sp):
            for sem in (s_ready, pT_dve, pT_act, o_ready):
                sp.sem_inc(sem, 1)
            tiles = sum(r[5] for r in runs)
            sp.wait_ge(o_done, tiles + 2)
            sp.dma_start(hbm["o_att"][:, :, 0:SEQ_S], qs[:, :].rearrange("p (h t) -> p h t", t=SEQ_S)).then_inc(out_done, 16)
            sp.dma_start(hbm["o_att"][:, :, SEQ_S:T], qp[:, :].rearrange("p (h t) -> p h t", t=SEQ_P)).then_inc(out_done, 16)
            sp.wait_ge(out_done, 32)


def shift_mix(dve, ch, out, src, mp, mn):
    for a, b in ((0, SEQ_S), (SEQ_S, T)):
        ch.then(dve.scalar_tensor_tensor(out[:, a + 1:b], src[:, a:b - 1], mp, out[:, a + 1:b], ALU.mult, ALU.add))
        ch.then(dve.scalar_tensor_tensor(out[:, a:b - 1], src[:, a + 1:b], mn, out[:, a:b - 1], ALU.mult, ALU.add))


def low_rank_stage(nc, hbm, xT, glob, low):
    with Stage(nc, "lr") as st:
        w = [st.sb(f"w{i}", 128, D) for i in range(3)]
        ps = st.psum()
        w_ready = st.sems("w0 w1 w2")
        z_ready, om_done, mixed, chain = st.sems("z_ready om_done mixed chain")
        block = st.block()

        @block.sync
        def _(sp):
            for c in range(3):
                sp.dma_start(w[c][:, :], hbm["w_in"][B_LOW + c]).then_inc(w_ready[c], 16)

        @block.tensor
        def _(pe):
            for c in range(3):
                pe.wait_ge(w_ready[c], 16)
                if c == 2:
                    pe.wait_ge(mixed, 1)
                dense_block(pe, ps, 3 * (c % 2), w[c], xT).then_inc(z_ready, 1)

        @block.scalar
        def _(act):
            for c in range(3):
                act.wait_ge(z_ready, c + 1)
                act.activation(low[c][:, :], set_of(ps, 3 * (c % 2)), ACT.Copy, scale=glob[:, G_OM + c:G_OM + c + 1]).then_inc(om_done, 1)
            act.wait_ge(mixed, 3)
            act.activation(low[0][:, :], low[0][:, :], ACT.Tanh).then_inc(om_done, 1)
            act.activation(low[2][:, :], low[2][:, :], ACT.Sigmoid).then_inc(om_done, 1)

        @block.vector
        def _(dve):
            ch = Chain(dve, chain)
            for c in range(3):
                dve.wait_ge(om_done, c + 1)
                shift_mix(dve, ch, low[c], set_of(ps, 3 * (c % 2)), glob[:, G_MP + c:G_MP + c + 1],
                          glob[:, G_MN + c:G_MN + c + 1])
                dve.sem_inc(mixed, 1)


def rwkv_stage(nc, hbm, xT, cst, low):
    with Stage(nc, "rw") as st:
        wv = [st.sb(f"w{i}", 128, D) for i in range(2)]
        wz = [st.sb(f"wz{i}", 128, D) for i in range(2)]
        lw = st.sb("lw", 128, 384)
        pc = [st.sb(f"pc{i}", 128, NPAIR + 5) for i in range(2)]
        resets = st.sb("resets", 128, GT)
        r, k, v, kh, bon, g, o, tq, ts = (st.sb(n, 128, T) for n in ("r", "k", "v", "kh", "bon", "g", "o", "tq", "ts"))
        a = [st.sb(f"a{d}", 128, T) for d in range(2)]
        kt = [k, st.sb("kt1", 128, T)]
        cw = [st.sb(f"cw{d}", 128, T) for d in range(2)]
        U8 = 2 * GRP
        P, Pi = st.sb("P", 128, U8, CH + 1), st.sb("Pi", 128, U8, CH + 1)
        vg = st.sb("vg", 128, GRP, CH)
        KQ = st.sb("KQ", 128, U8, 3 * CH)
        Kg, AKg = st.sb("Kg", 128, GRP, 2 * CH), st.sb("AKg", 128, GRP, 2 * CH)
        lg = st.sb("lg", 128, 2, GT)
        Vt, Kt = st.sb("Vt", 128, U8, CH), st.sb("Kt", 128, U8, CH)
        AKt = st.sb("AKt", 128, U8, CH)
        SAB, SAK = st.sb("SAB", 128, U8, 2 * CH), st.sb("SAK", 128, U8, 2 * CH)
        LT, M, N, X = (st.sb(n, 128, 2, GRP * 32) for n in ("LT", "M", "N", "X"))
        NF = st.sb("NF", 128, U8, CH)
        ST, STp, Bs, Us = (st.sb(n, 128, 2, CH) for n in ("ST", "STp", "Bs", "Us"))
        ps = st.psum()
        A1, A2, BU, OB, ZN, LG = 0, 2, 4, 5, 6, 7
        T1, T2 = A1, A1 + 1

        def two(name):
            return st.sems(f"{name}0 {name}1")

        vw_ready, lw_ready, pc_ready, om_ready = st.sems("vw_ready lw_ready pc_ready om_ready")
        low_ready, low_done, k_ready, r_ready, v_ready, ss_ready, g_ready, bonus_ready = st.sems(
            "low_ready low_done k_ready r_ready v_ready ss_ready g_ready bonus_ready")
        om_done, k_mixed, r_mixed, v_mixed, sqk_done, rt_done, kh_done, scan_done = st.sems(
            "om_done k_mixed r_mixed v_mixed sqk_done rt_done kh_done scan_done")
        asum, asc, ask, bsum, bonus_done, g_done, set_up = st.sems("asum asc ask bsum bonus_done g_done set_up")
        mean_ready, oc_done, osq_done, var_ready, std_done, out_ready, out_sent, o_zero = st.sems(
            "mean_ready oc_done osq_done var_ready std_done out_ready out_sent o_zero")
        exp_done, vg_ready, kq_ready, kg_ready = (two(n) for n in ("exp_done", "vg_ready", "kq_ready", "kg_ready"))
        kt_scale, kt_done, ak_done = st.sems("kt_scale kt_done ak_done")
        zw_ready, gw_ready, lg_sent = (two(n) for n in ("zw_ready", "gw_ready", "lg_sent"))
        zn_ready, zn_copied, lz_ready, lz_copied, z0_copied = st.sems("zn_ready zn_copied lz_ready lz_copied z0_copied")
        t_ready, tev, masked, mn_ready, x_ready, xe_ready, mx_ready = (two(n) for n in (
            "t_ready", "tev", "masked", "mn_ready", "x_ready", "xe_ready", "mx_ready"))
        x21_ready, x21e, n12_ready, nf_ready, state_ready = (two(n) for n in (
            "x21_ready", "x21e", "n12_ready", "nf_ready", "state_ready"))
        b_ready, be, u_ready, ue, s_ready, o_added = (two(n) for n in ("b_ready", "be", "u_ready", "ue", "s_ready", "o_added"))
        c_pair, c_end, ln_ss, ln_var, passed = st.sems("c_pair c_end ln_ss ln_var passed")
        c_prep, c_scan, c_mask = two("c_prep"), two("c_scan"), two("c_mask")
        ident64, bones = cst[:, C_ID64:C_ID64 + 64], cst[:, C_BONES:C_BONES + 128]
        id32, sel0, sel1 = cst[:, C_ID32:C_ID32 + 32], cst[:, C_SEL:C_SEL + 1], cst[:, C_SEL + 1:C_SEL + 2]
        LVL = 4

        def level(d, l):
            at = C_LVL + 160 * d + 32 * l
            return cst[:, at:at + 32].unsqueeze(1).broadcast_to([128, GRP, 32])

        def units(x, d, n=32):
            return x[:, d, :].rearrange("p (u n) -> p u n", n=n)

        def of(d):
            return slice(GRP * d, GRP * d + GRP)

        def scores_at(bank, c, n):
            return ps[:, bank:bank + 2, 0:384].rearrange("p b (u n) -> p b u n", n=192)[:, :, :, c:c + n]

        def four(x):
            return x.rearrange("p (b u) n -> p b u n", b=2)

        def first(d, s):
            return s * GT if d == 0 else s * -GT + GT * (STEPS - 1)

        def tok(x, d, s):
            return x[:, bass.ds(first(d, s), GT)].rearrange("p (u n) -> p u n", n=CH)

        def incl(x, d):
            return x[:, of(d), 1:CH + 1]

        def excl(x, d):
            return x[:, of(d), 0:CH]

        SLOTS = {(0, 1): 0, (0, 2): 1, (1, 1): 2, (1, 2): 3, (2, 0): 4, (2, 1): 5, (2, 2): 6, (3, 0): 7, (3, 1): 8, (3, 2): 9}

        FILLS = (3, 1, 0, 0, 4, 1, 1, 1, 1, 1, 1, 1, 0, 0, 1)

        def phase(link, part, fill=None):
            def fills(at):
                if fill:
                    for i in range(FILLS[at]):
                        fill(sum(FILLS[:at]) + i)

            fills(0)
            for c in range(GRP):
                for kind in range(3):
                    if link:
                        link(c, kind)
                    fills(1 + 3 * c + kind)
                    if part and (c, kind) in SLOTS:
                        part(SLOTS[c, kind])
            if part:
                for i in range(len(SLOTS), 12):
                    if i >= 10:
                        fills(3 + i)
                    part(i)

        def group_loop(eng, p, more, both):
            both(p, more, (0, 0), None)
            both(p, more, (1, 0), (0, 0))
            with eng.Fori(1, STEPS, 1) as s:
                both(p, more, (0, s), (1, s + -1))
                both(p, more, (1, s), (0, s))
            both(p, more, None, (1, STEPS - 1))

        def pair_loop(eng, projections, both, norm):
            projections(0)
            with eng.Fori(0, PAIRS - 1, 1) as p:
                group_loop(eng, p, True, both)
                norm(p, True)
            group_loop(eng, PAIRS - 1, False, both)
            norm(PAIRS - 1, False)

        block = st.block()

        @block.sync
        def _(sp):
            for sem in (out_ready, out_sent, o_added[0], o_added[1], low_done, bonus_done,
                        zn_copied, lz_copied, lg_sent[0], lg_sent[1]):
                sp.sem_inc(sem, 1)

            def row(x, i):
                return x[bass.ds(i, 1), :, :].rearrange("a p n -> (a p) n")

            def loads(p, more):
                sp.wait_ge(v_ready, p + 1)
                settle(sp, passed)
                sp.dma_start(wv[0][:, :], row(hbm["w_gate"], p * 2)).then_inc(gw_ready[0], 16)
                if more:
                    for c, b in enumerate((B_K, B_R)):
                        sp.dma_start(wz[c][:, :], row(hbm["w_in"], p + (b + 1))).then_inc(zw_ready[c], 16)
                    sp.wait_ge(bonus_done, p + 2)
                    settle(sp, passed)
                    sp.dma_start(lw[:, :], row(hbm["w_low"], p + 1)).then_inc(lw_ready, 16)
                    sp.dma_start(pc[1][:, 0:NPAIR], row(hbm["pcols"], p + 1)).then_inc(pc_ready, 16)
                with sp.Fori(0, STEPS, 1) as i:
                    for d in range(2):
                        sp.wait_ge(lz_copied, p * (2 * STEPS) + i * 2 + (d + 2))
                        settle(sp, passed)
                        sp.dma_start(row(hbm["logits"], p * 2 + d)[:, bass.ds(i * GT, GT)], lg[:, d, :]).then_inc(lg_sent[d], 16)
                if more:
                    sp.dma_start(wv[0][:, :], row(hbm["w_in"], p + (B_V + 1))).then_inc(vw_ready, 16)
                    sp.dma_start(wv[1][:, :], row(hbm["w_gate"], p * 2 + 3)).then_inc(gw_ready[1], 16)

            def send(p, q):
                sp.wait_ge(out_ready, q + 2)
                settle(sp, passed)
                sp.dma_start(hbm["o_rw"][:, bass.ds(p, 1), :].rearrange("p a t -> p (a t)"), g[:, :]).then_inc(out_sent, 16)

            sp.dma_start(lw[:, :], hbm["w_low"][0]).then_inc(lw_ready, 16)
            sp.dma_start(pc[1][:, 0:NPAIR], hbm["pcols"][0]).then_inc(pc_ready, 16)
            for c, b in enumerate((B_K, B_R)):
                sp.dma_start(wz[c][:, :], hbm["w_in"][b]).then_inc(zw_ready[c], 16)
            sp.dma_start(wv[0][:, :], hbm["w_in"][B_V]).then_inc(vw_ready, 16)
            sp.dma_start(wv[1][:, :], hbm["w_gate"][1]).then_inc(gw_ready[1], 16)
            with sp.Fori(0, PAIRS - 1, 1) as p:
                loads(p, True)
                send(p, p)
            loads(PAIRS - 1, False)
            sp.wait_ge(out_ready, PAIRS + 1)
            sp.dma_start(hbm["o_rw"][:, PAIRS - 1, :], g[:, :]).then_inc(out_sent, 16)
            sp.wait_ge(out_sent, 16 * PAIRS + 1)
            for d in range(2):
                sp.wait_ge(lg_sent[d], 16 * PAIRS * STEPS + 1)

        @block.tensor
        def _(pe):
            def quads(out, lhsT, rhs):
                for h in (0, 64):
                    last = pe.matmul(out[h:h + 64], lhsT[h:h + 64], rhs[h:h + 64], start=True, stop=True)
                return last

            def accumulate(out, terms):
                for i, (lhsT, rhs) in enumerate(terms):
                    for h in (0, 64):
                        last = pe.matmul(out[h:h + 64], lhsT[h:h + 64], rhs[h:h + 64], start=(i == 0), stop=(i == len(terms) - 1))
                return last

            def diag32(bank, d, lhsT, rhs):
                for u in range(GRP):
                    for q in range(4):
                        at, c = 32 * q, 32 * u
                        last = pe.matmul(ps[at:at + 32, bank, c:c + 32], lhsT[at:at + 32, d, c:c + 32],
                                         rhs[at:at + 32, d, c:c + 32], start=True, stop=True)
                return last

            def corner(bank, d, src, dst, lhsT, rhs):
                for u in range(GRP):
                    for h in (0, 64):
                        i, j = h + src, h + dst
                        last = pe.matmul(ps[j:j + 32, bank, 32 * u:32 * u + 32], lhsT(u)[i:i + 32], rhs[i:i + 32, d, 32 * u:32 * u + 32],
                                         start=True, stop=True)
                return last

            def both(p, more, prep, scan):
                def part(i):
                    d, s = prep
                    n = p * STEPS + s
                    if i == 0:
                        pe.wait_ge(vg_ready[d], n + 1)
                        pe.wait_ge(kg_ready[d], n * 4 + 4)
                        pe.wait_ge(kq_ready[d], n * 2 + 2)
                        settle(pe, passed)
                    if i <= 1:
                        for u in (2 * i, 2 * i + 1):
                            q = GRP * d + u
                            b, c = i, 192 * (u % 2)
                            pe.matmul(ps[:, A1 + b, c:c + 192], AKg[:, u, :], KQ[:, q, :], start=True, stop=True)
                            pe.matmul(ps[:, A2 + b, c:c + 192], Kg[:, u, :], KQ[:, q, :], start=True, stop=True)
                            c = 384 + CH * (u % 2)
                            last = quads(ps[:, A1 + b, c:c + CH], vg[:, u, :], ident64)
                        last.then_inc(t_ready[d], 1)
                    elif i <= 9:
                        l = (i - 2) // 2
                        if i % 2 == 0:
                            if l == 0:
                                pe.wait_ge(tev[d], n * 3 + 3)
                            pe.wait_ge(mn_ready[d], n * 5 + l + 1)
                            settle(pe, passed)
                            diag32(T1, d, LT, M).then_inc(x_ready[d], 1)
                        else:
                            pe.wait_ge(xe_ready[d], n * 4 + l + 1)
                            settle(pe, passed)
                            diag32(T2, d, N, X).then_inc(mx_ready[d], 1)
                    elif i == 10:
                        pe.wait_ge(mn_ready[d], n * 5 + 5)
                        settle(pe, passed)
                        src, dst = (0, 32) if d == 0 else (32, 0)
                        corner(T1, d, src, dst, lambda u: SAB[:, GRP * d + u, dst:dst + 32], M).then_inc(x21_ready[d], 1)
                    else:
                        pe.wait_ge(x21e[d], n * 2 + 2)
                        settle(pe, passed)
                        src, dst = (32, 0) if d == 0 else (0, 32)
                        corner(T2, d, src, dst, lambda u: X[:, d, 32 * u:32 * u + 32], N).then_inc(n12_ready[d], 1)

                def link(c, kind):
                    d, s = scan
                    n = p * STEPS + s
                    j = c if d == 0 else GRP - 1 - c
                    u, S = GRP * d + j, (ST, STp)[d]
                    V, K = Vt[:, u, :], Kt[:, u, :]
                    if kind == 0:
                        if c == 0:
                            pe.wait_ge(nf_ready[d], n * 2 + 2)
                            pe.wait_ge(o_added[1 - d], n + 2 if d else n + 1)
                        pe.wait_ge(state_ready[d], n * GRP + c + 1)
                        settle(pe, passed)
                        accumulate(ps[:, BU, 0:64], [(SAK[:, u, 0:64], V), (KQ[:, u, 0:64], S[:, d, :])]).then_inc(b_ready[d], 1)
                    elif kind == 1:
                        pe.wait_ge(be[d], n * GRP + c + 1)
                        settle(pe, passed)
                        quads(ps[:, BU, 64:128], NF[:, u, :], Bs[:, d, :]).then_inc(u_ready[d], 1)
                    else:
                        pe.wait_ge(ue[d], n * GRP + c + 1)
                        settle(pe, passed)
                        accumulate(ps[:, OB, 64 * j:64 * j + 64], [(S[:, d, :], KQ[:, u, 64:128]), (V, SAK[:, u, 64:128]),
                                                                   (Us[:, d, :], SAB[:, u, 64:128])])
                        accumulate(ps[:, BU, 128:192], [(K, V), (AKt[:, u, :], Us[:, d, :])]).then_inc(s_ready[d], 1)

                def fill(i):
                    d, s = prep
                    m = p * (2 * STEPS) + s * 2 + d
                    gate, k = i >= KT, i % KT
                    if not gate and not more:
                        return
                    if k == 0:
                        if gate:
                            pe.wait_ge(gw_ready[d], p * 16 + 16)
                        else:
                            pe.wait_ge(zw_ready[d], p * 16 + 32)
                        pe.wait_ge(lz_copied if gate else zn_copied, m + 1)
                        settle(pe, passed)
                    weights = (wv if gate else wz)[d]
                    last = pe.matmul(ps[:, LG if gate else ZN, 0:GT], weights[:, 128 * k:128 * k + 128],
                                     xT[:, k, bass.ds(s * GT, GT)], start=(k == 0), stop=(k == KT - 1))
                    if k == KT - 1:
                        last.then_inc(lz_ready if gate else zn_ready, 1)

                phase(scan and link, prep and part, prep and fill)

            def projections(p, norm=None):
                pe.wait_ge(lw_ready, p * 16 + 16)
                if norm is not None:
                    pe.wait_ge(o_added[0], norm * STEPS + STEPS + 1)
                    pe.wait_ge(o_added[1], norm * STEPS + STEPS + 1)
                    settle(pe, passed)
                wide(pe, ps, 0, lw[0:64, 0:128], low[0][0:64]).then_inc(low_ready, 1)
                wide(pe, ps, 3, lw[64:128, 0:128], low[0][64:128]).then_inc(low_ready, 1)
                pe.wait_ge(low_done, p * 4 + 2)
                settle(pe, passed)
                wide(pe, ps, 0, lw[0:64, 128:256], low[1][0:64]).then_inc(low_ready, 1)
                pe.wait_ge(low_done, p * 4 + 3)
                settle(pe, passed)
                wide(pe, ps, 3, lw[64:128, 128:256], low[1][64:128]).then_inc(low_ready, 1)
                if norm is None:
                    pe.wait_ge(low_done, p * 4 + 4)
                    pe.wait_ge(zw_ready[0], 16)
                    dense_block(pe, ps, 0, wz[0], xT).then_inc(k_ready, 1)
                    pe.wait_ge(low_done, p * 4 + 5)
                    pe.wait_ge(zw_ready[1], 16)
                    dense_block(pe, ps, 3, wz[1], xT).then_inc(k_ready, 1)
                    pe.wait_ge(z0_copied, 2)
                else:
                    pe.wait_ge(low_done, p * 4 + 4)
                    settle(pe, passed)
                    wide(pe, ps, 0, bones, o).then_inc(mean_ready, 1)
                pe.wait_ge(vw_ready, p * 16 + 16)
                pe.wait_ge(low_done, p * 4 + 5)
                dense_block(pe, ps, 3, wv[0], xT).then_inc(v_ready, 1)
                pe.wait_ge(sqk_done, p + 1)
                if norm is not None:
                    pe.wait_ge(oc_done, norm + 1)
                    settle(pe, passed)
                wide(pe, ps, 0, bones, tq).then_inc(ss_ready, 1)
                pe.wait_ge(rt_done, p + 1)
                if norm is not None:
                    pe.wait_ge(osq_done, norm + 1)
                    wide(pe, ps, 0, bones, tq).then_inc(var_ready, 1)
                pe.wait_ge(v_mixed, p + 1)
                settle(pe, passed)
                wide(pe, ps, 3, lw[:, 256:384], low[2]).then_inc(g_ready, 1)
                if norm is not None:
                    pe.wait_ge(std_done, norm + 1)
                pe.wait_ge(bsum, p + 1)
                wide(pe, ps, 0, bones, bon).then_inc(bonus_ready, 1)
                pe.wait_ge(g_done, p + 1)
                pe.wait_ge(bonus_done, p + 2)
                settle(pe, passed)

            def norm(p, more):
                if more:
                    projections(p + 1, p)
                    return
                pe.wait_ge(o_added[0], p * STEPS + STEPS + 1)
                pe.wait_ge(o_added[1], p * STEPS + STEPS + 1)
                wide(pe, ps, 0, bones, o).then_inc(mean_ready, 1)
                pe.wait_ge(osq_done, p + 1)
                wide(pe, ps, 0, bones, tq).then_inc(var_ready, 1)

            pair_loop(pe, projections, both, norm)

        @block.scalar
        def _(act):
            def both(p, more, prep, scan):
                if prep:
                    d, s = prep
                    n = p * STEPS + s
                    act.wait_ge(o_added[d], n + 1)
                    act.wait_ge(scan_done, p * (2 * STEPS) + 2 * STEPS)
                    src = tok(cw[d], d, s)
                    act.activation(incl(Pi, d), src, ACT.Exp, scale=DECAY_SCALE).then_inc(exp_done[d], 1)
                    act.activation(incl(P, d), src, ACT.Exp, scale=-DECAY_SCALE).then_inc(exp_done[d], 1)
                    act.wait_ge(v_mixed, p + 1)
                    act.wait_ge(t_ready[1 - d], n * 2 + (1 if d == 0 else 3))
                    act.activation(vg[:, :, :], tok(v, d, s), ACT.Copy).then_inc(vg_ready[d], 1)

                def part(i):
                    if i == 1:
                        act.wait_ge(t_ready[d], n * 2 + 3)
                        act.activation(four(Kt[:, of(d), :]), scores_at(A2, 128, 64), ACT.Copy).then_inc(tev[d], 1)
                        act.wait_ge(masked[d], n + 1)
                        act.activation(four(AKt[:, of(d), :]), scores_at(A1, 128, 64), ACT.Copy, scale=-1.0).then_inc(tev[d], 1)
                        act.activation(four(Vt[:, of(d), :]), ps[:, A1:A1 + 2, 384:512].rearrange("p b (u n) -> p b u n", n=CH),
                                       ACT.Copy).then_inc(tev[d], 1)
                    elif i == 4 and more:
                        act.wait_ge(zn_ready, p * (2 * STEPS) + s * 2 + (d + 1))
                        act.wait_ge(kt_done, p * 2 + 2)
                        settle(act, passed)
                        act.activation((tq, ts)[d][:, bass.ds(s * GT, GT)], ps[:, ZN, 0:GT], ACT.Copy).then_inc(zn_copied, 1)
                    elif i == 11:
                        act.wait_ge(lz_ready, p * (2 * STEPS) + s * 2 + (d + 1))
                        act.wait_ge(lg_sent[d], n * 16 + 1)
                        settle(act, passed)
                        act.activation(lg[:, d, :], ps[:, LG, 0:GT], ACT.Copy).then_inc(lz_copied, 1)

                def link(c, kind):
                    ds, ss = scan
                    m = p * STEPS + ss
                    if kind == 0:
                        act.wait_ge(b_ready[ds], m * GRP + c + 1)
                        act.activation(Bs[:, ds, :], ps[:, BU, 0:64], ACT.Copy).then_inc(be[ds], 1)
                    elif kind == 1:
                        act.wait_ge(u_ready[ds], m * GRP + c + 1)
                        act.activation(Us[:, ds, :], ps[:, BU, 64:128], ACT.Copy).then_inc(ue[ds], 1)

                phase(scan and link, prep and part)

            def projections(p, norm=None):
                c = pc[1]
                act.wait_ge(pc_ready, p * 16 + 16)
                if norm is not None:
                    act.wait_ge(o_added[0], norm * STEPS + STEPS + 1)
                    act.wait_ge(o_added[1], norm * STEPS + STEPS + 1)
                act.wait_ge(om_ready, p + 1)
                def own(dst, z, column):
                    act.activation(dst[:, :], z, ACT.Copy, scale=c[:, column:column + 1]).then_inc(om_done, 1)

                if norm is not None:
                    act.wait_ge(zn_copied, norm * (2 * STEPS) + (2 * STEPS + 1))
                    settle(act, passed)
                    own(k, tq[:, :], P_OM + 1)
                    own(r, ts[:, :], P_OM)
                for j, (dst, b) in enumerate(((cw[0], P_W0), (cw[1], P_W0 + 1), (a[0], P_A0), (a[1], P_A0 + 1))):
                    act.wait_ge(low_ready, p * 4 + j + 1)
                    act.activation(dst[:, :], set_of(ps, 3 * (j % 2)), ACT.Sigmoid, bias=c[:, b:b + 1]).then_inc(low_done, 1)
                if norm is None:
                    for j, z in enumerate((tq, ts)):
                        act.wait_ge(k_ready, j + 1)
                        act.activation(z[:, :], set_of(ps, 3 * j), ACT.Copy).then_inc(z0_copied, 1)
                    act.wait_ge(z0_copied, 2)
                    own(k, tq[:, :], P_OM + 1)
                    own(r, ts[:, :], P_OM)
                act.wait_ge(k_mixed, p + 1)
                act.activation(tq[:, :], k[:, :], ACT.Square, scale=c[:, P_KK:P_KK + 1]).then_inc(sqk_done, 1)
                act.wait_ge(v_ready, p + 1)
                own(v, set_of(ps, 3), P_OM + 2)
                act.wait_ge(ss_ready, p + 1)
                act.activation(kh[:, :], set_of(ps, 0), ACT.Ln).then_inc(ln_ss, 1)
                act.wait_ge(ln_ss, p + 1)
                settle(act, passed)
                act.activation(kh[:, :], kh[:, :], ACT.Exp, scale=-0.5).then_inc(rt_done, 1)
                if norm is not None:
                    act.wait_ge(r_mixed, p + 1)
                    square_norm(norm)
                act.wait_ge(g_ready, p + 1)
                if norm is not None:
                    act.wait_ge(out_sent, norm * 16 + 17)
                act.activation(g[:, :], set_of(ps, 3), ACT.Copy).then_inc(g_done, 1)

            def square_norm(p):
                act.wait_ge(oc_done, p + 1)
                act.activation(tq[:, :], o[:, :], ACT.Square).then_inc(osq_done, 1)
                act.wait_ge(var_ready, p + 1)
                act.activation(ts[:, :], set_of(ps, 0), ACT.Ln, bias=cst[:, C_EPS + 1:C_EPS + 2], scale=1.0 / CH).then_inc(ln_var, 1)
                act.wait_ge(ln_var, p + 1)
                settle(act, passed)
                act.activation(ts[:, :], ts[:, :], ACT.Exp, scale=-0.5).then_inc(std_done, 1)

            def norm(p, more):
                if more:
                    projections(p + 1, p)
                else:
                    square_norm(p)

            pair_loop(act, projections, both, norm)

        @block.gpsimd
        def _(pool):
            for x in (P, Pi):
                pool.memset(x[:, :, 0:1], 1.0).then_inc(set_up, 1)
            for x, value in ((resets, 1.0), (ST, 0.0), (Kg, 0.0), (AKg, 0.0)):
                pool.memset(x[tuple(slice(None) for _ in x.shape)], value).then_inc(set_up, 1)
            pool.tensor_copy(KQ[:, :, 2 * CH:3 * CH], ident64.unsqueeze(1).broadcast_to([128, U8, CH])).then_inc(set_up, 1)
            pool.wait_ge(set_up, 7)
            pool.memset(resets[:, :].rearrange("p (c n) -> p c n", n=CH)[:, :, 0:1], 0.0).then_inc(set_up, 1)

            def both(p, more, prep, scan):
                if not prep:
                    return
                d, s = prep
                n = p * STEPS + s
                pool.wait_ge(o_added[d], n + 1)
                pool.wait_ge(exp_done[d], n * 2 + 2)
                pool.tensor_tensor(KQ[:, of(d), 0:CH], tok(kh, d, s), excl(P, 0) if d == 0 else incl(Pi, 1),
                                   ALU.mult).then_inc(kq_ready[d], 1)
                pool.tensor_tensor(KQ[:, of(d), CH:2 * CH], tok(r, d, s), incl(P, 0) if d == 0 else excl(Pi, 1),
                                   ALU.mult).then_inc(kq_ready[d], 1)

            def projections(p, norm=None):
                pool.wait_ge(low_done, p * 4 + 5)
                if norm is not None:
                    pool.wait_ge(out_ready, norm + 2)
                pool.wait_ge(r_mixed, p + 1)
                pool.tensor_tensor(ts[:, :], a[0][:, :], a[1][:, :], ALU.add).then_inc(asum, 1)
                pool.memset(o[:, :], 0.0).then_inc(o_zero, 1)
                pool.wait_ge(asc, p + 1)
                pool.wait_ge(k_mixed, p + 1)
                pool.tensor_tensor(bon[:, :], ts[:, :], k[:, :], ALU.mult).then_inc(ask, 1)
                pool.wait_ge(kt_scale, p * 2 + 1)
                pool.tensor_tensor(kt[1][:, :], ts[:, :], k[:, :], ALU.mult).then_inc(kt_done, 1)
                pool.wait_ge(kt_scale, p * 2 + 2)
                pool.wait_ge(kt_done, p * 2 + 1)
                pool.tensor_tensor(kt[0][:, :], tq[:, :], k[:, :], ALU.mult).then_inc(kt_done, 1)

            pool.sem_inc(t_ready[0], 1)
            pool.sem_inc(t_ready[1], 1)
            pair_loop(pool, projections, both,
                      lambda p, more: projections(p + 1, p) if more else None)

        @block.vector
        def _(dve):
            def both(p, more, prep, scan):
                if prep:
                    d, s = prep
                    n = p * STEPS + s
                    cp = Chain(dve, c_prep[d], n * LEN_PREP)
                    dec = incl(Pi, 0) if d == 0 else excl(P, 1)
                    dve.wait_ge(t_ready[1 - d], n * 2 + (1 if d == 0 else 3))
                    dve.wait_ge(kt_done, p * 2 + 2)
                    dve.wait_ge(ak_done, p * 2 + 2)
                    dve.wait_ge(exp_done[d], n * 2 + 2)
                    for dst, src in ((Kg, kt[d]), (AKg, a[d])):
                        x = tok(src, d, s)
                        for h in (0, 64):
                            dve.tensor_tensor(dst[h:h + 64, :, h:h + 64], x[h:h + 64], dec[h:h + 64], ALU.mult).then_inc(kg_ready[d], 1)
                if scan:
                    e, ss = scan
                    m = p * STEPS + ss
                    cs = Chain(dve, c_scan[e], m * (LEN_F, LEN_B)[e])
                    flag = cst[:, bass.ds(ss + (C_FLAG + STEPS * e), 1)]
                    if e == 0:
                        dve.tensor_scalar(ST[:, 0, :], ST[:, 0, :], flag, None, ALU.mult).then_inc(state_ready[0], 1)
                    else:
                        dve.tensor_scalar(STp[:, 1, :], ST[:, 1, :], flag, P[:, U8 - 1, CH:CH + 1], ALU.mult, ALU.mult).then_inc(state_ready[1], 1)

                def part(i):
                    if i == 1:
                        dve.wait_ge(t_ready[d], n * 2 + 3)
                        for buf, bank, mask in ((SAB, A1, C_MAB), (SAK, A2, C_MAK)):
                            m = cst[:, mask + 128 * d:mask + 128 * d + 128].unsqueeze(1).unsqueeze(1).broadcast_to([128, 2, 2, 128])
                            if bank == A2:
                                dve.wait_ge(tev[d], n * 3 + 1)
                            dve.tensor_tensor(four(buf[:, of(d), :]), scores_at(bank, 0, 128), m, ALU.mult).then_inc((masked if bank == A1 else c_mask)[d], 1)
                        dve.wait_ge(masked[d], n + 1)
                        dve.wait_ge(c_mask[d], n + 1)
                        cp.then(dve.tensor_scalar(units(N, d), SAB[:, of(d), 0:32], sel0, None, ALU.mult))
                        cp.then(dve.scalar_tensor_tensor(units(LT, d), SAB[:, of(d), 32:64], sel1, units(N, d), ALU.mult, ALU.add))
                        cp.then(dve.tensor_tensor(units(N, d), units(LT, d), level(d, 0), ALU.mult))
                        cp.then(dve.tensor_tensor(units(N, d), units(N, d), id32.unsqueeze(1).broadcast_to([128, GRP, 32]), ALU.add))
                        dve.transpose(M[:, d, :], N[:, d, :]).then_inc(mn_ready[d], 1)
                    elif 2 <= i <= 9:
                        l = (i - 2) // 2
                        if i % 2 == 0:
                            dve.wait_ge(x_ready[d], n * 4 + l + 1)
                            dve.tensor_tensor(units(X, d), ps[:, T1, 0:128].rearrange("p (u n) -> p u n", n=32), level(d, l + 1),
                                              ALU.mult).then_inc(xe_ready[d], 1)
                        else:
                            dve.wait_ge(mx_ready[d], n * 4 + l + 1)
                            dve.wait_ge(mn_ready[d], n * 5 + l + 1)
                            cp.then(dve.tensor_tensor(M[:, d, :], ps[:, T2, 0:128], M[:, d, :], ALU.add))
                            dve.transpose(N[:, d, :], M[:, d, :]).then_inc(mn_ready[d], 1)
                    elif i == 10:
                        dve.wait_ge(x21_ready[d], n + 1)
                        at = 32 if d == 0 else 0
                        for h in (0, 64):
                            dve.tensor_scalar(X[h + at:h + at + 32, d, :], ps[h + at:h + at + 32, T1, 0:128], -1.0, None,
                                              ALU.mult).then_inc(x21e[d], 1)
                        dve.wait_ge(mn_ready[d], n * 5 + 5)
                        cp.then(dve.tensor_tensor(NF[:, of(d), :].rearrange("p u (j n) -> p u j n", n=32),
                                                  units(N, d).unsqueeze(2).broadcast_to([128, GRP, 2, 32]),
                                                  cst[:, C_BLK:C_BLK + 64].rearrange("p (j n) -> p j n", n=32).unsqueeze(1).broadcast_to([128, GRP, 2, 32]),
                                                  ALU.mult))
                    elif i == 11:
                        at = 0 if d == 0 else 32
                        dve.wait_ge(n12_ready[d], n + 1)
                        for h in (0, 64):
                            dve.tensor_copy(NF[h + at:h + at + 32, of(d), 32 - at:64 - at],
                                            ps[h + at:h + at + 32, T2, 0:128].rearrange("p (u n) -> p u n", n=32)).then_inc(nf_ready[d], 1)

                def link(c, kind):
                    pu = P[:, c:c + 1, CH:CH + 1].rearrange("p a b -> p (a b)") if e == 0 else \
                        P[:, U8 - 2 - c:U8 - 1 - c, CH:CH + 1].rearrange("p a b -> p (a b)")
                    if kind == 0 and e == 0:
                        dve.wait_ge(state_ready[0], m * GRP + c + 1)
                        cs.then(dve.tensor_scalar(STp[:, 0, :], ST[:, 0, :], pu, None, ALU.mult))
                    if kind != 2:
                        return
                    dve.wait_ge(s_ready[e], m * GRP + c + 1)
                    if e == 0:
                        up = dve.scalar_tensor_tensor(ST[:, 0, :], ps[:, BU, 128:192], pu, STp[:, 0, :], ALU.mult, ALU.add)
                        up.then_inc(state_ready[0], 1) if c < GRP - 1 else cs.then(up)
                    else:
                        dve.wait_ge(state_ready[1], m * GRP + c + 1)
                        cs.then(dve.tensor_tensor(ST[:, 1, :], ps[:, BU, 128:192], STp[:, 1, :], ALU.add))
                        if c < GRP - 1:
                            dve.tensor_scalar(STp[:, 1, :], ST[:, 1, :], pu, None, ALU.mult).then_inc(state_ready[1], 1)
                    if c == GRP - 1:
                        dve.wait_ge(o_zero, p + 1)
                        dve.wait_ge(o_added[1 - e], m + 2 if e else m + 1)
                        dst = o[:, bass.ds(first(e, ss), GT)]
                        dve.tensor_tensor(dst, ps[:, OB, 0:GT], dst, ALU.add).then_inc(o_added[e], 1)

                phase(scan and link, prep and part)
                if prep:
                    assert cp.n == LEN_PREP, cp.n
                if scan:
                    assert cs.n == (LEN_F, LEN_B)[e], cs.n

            def projections(p, norm=None):
                ch = Chain(dve, c_pair, p * LEN_PAIR)
                c = pc[1]
                dve.wait_ge(pc_ready, p * 16 + 16)
                om = c[:, P_OM:P_OM + 3]
                ch.then(dve.tensor_tensor(om, c[:, P_MP:P_MP + 3], c[:, P_MN:P_MN + 3], ALU.add))
                ch(dve.tensor_scalar(om, om, -1.0, 1.0, ALU.mult, ALU.add))
                ch(dve.tensor_scalar(c[:, P_OKA:P_OKA + 1], c[:, P_KA:P_KA + 1], -1.0, 1.0, ALU.mult, ALU.add))
                ch.then(dve.tensor_scalar(c[:, P_OKA2:P_OKA2 + 1], c[:, P_KA:P_KA + 1], -2.0, 2.0, ALU.mult, ALU.add))
                dve.sem_inc(om_ready, 1)
                dve.wait_ge(set_up, 8)

                def mix(x, i, j, z, done):
                    dve.wait_ge(om_done, p * 3 + i + 1)
                    shift_mix(dve, ch, x, z, c[:, P_MP + j:P_MP + j + 1], c[:, P_MN + j:P_MN + j + 1])
                    dve.sem_inc(done, 1)

                mix(k, 0, 1, tq, k_mixed)
                mix(r, 1, 0, ts, r_mixed)
                for d in range(2):
                    dve.wait_ge(low_done, p * 4 + d + 2)
                    for t in range(0, T, GT):
                        dve.tensor_tensor_scan(cw[d][:, t:t + GT], resets[:, :], cw[d][:, t:t + GT], 0.0,
                                               ALU.mult, ALU.add).then_inc(scan_done, 1)
                if norm is not None:
                    centre(norm)
                mix(v, 2, 2, set_of(ps, 3), v_mixed)
                dve.wait_ge(rt_done, p + 1)
                ch.then(dve.scalar_tensor_tensor(kh[:, :], kh[:, :], 1e12, k[:, :], ALU.min, ALU.mult))
                dve.tensor_scalar(kh[:, :], kh[:, :], c[:, P_KK:P_KK + 1], None, ALU.mult).then_inc(kh_done, 1)
                if norm is not None:
                    scale_norm(norm)
                ch(dve.tensor_copy(pc[0][:, :], c[:, :]))
                dve.wait_ge(asum, p + 1)
                dve.tensor_scalar(ts[:, :], ts[:, :], c[:, P_KA:P_KA + 1], c[:, P_OKA2:P_OKA2 + 1], ALU.mult, ALU.add).then_inc(asc, 1)
                dve.wait_ge(ask, p + 1)
                dve.scalar_tensor_tensor(bon[:, :], bon[:, :], c[:, P_RK:P_RK + 1], r[:, :], ALU.mult, ALU.mult).then_inc(bsum, 1)
                dve.wait_ge(ask, p + 1)
                dve.tensor_scalar(ts[:, :], a[1][:, :], c[:, P_KA:P_KA + 1], c[:, P_OKA:P_OKA + 1], ALU.mult, ALU.add).then_inc(kt_scale, 1)
                if norm is not None:
                    dve.wait_ge(std_done, norm + 1)
                dve.wait_ge(ss_ready, p + 1)
                dve.tensor_scalar(tq[:, :], a[0][:, :], c[:, P_KA:P_KA + 1], c[:, P_OKA:P_OKA + 1], ALU.mult, ALU.add).then_inc(kt_scale, 1)
                dve.wait_ge(kh_done, p + 1)
                dve.wait_ge(kt_scale, p * 2 + 2)
                for d in range(2):
                    dve.tensor_tensor(a[d][:, :], a[d][:, :], kh[:, :], ALU.mult).then_inc(ak_done, 1)
                dve.wait_ge(bonus_ready, p + 1)
                dve.tensor_tensor(bon[:, :], set_of(ps, 0), v[:, :], ALU.mult).then_inc(bonus_done, 1)
                dve.wait_ge(bonus_done, p + 2)
                ch.sync()
                settle(dve, passed)
                assert ch.n == LEN_PAIR, ch.n

            def centre(p):
                dve.wait_ge(mean_ready, p + 1)
                dve.scalar_tensor_tensor(o[:, :], set_of(ps, 0), -1.0 / CH, o[:, :], ALU.mult, ALU.add).then_inc(oc_done, 1)

            def scale_norm(p):
                ch = Chain(dve, c_end, p * LEN_END)
                dve.wait_ge(std_done, p + 1)
                dve.wait_ge(oc_done, p + 1)
                dve.wait_ge(bonus_done, p + 2)
                ch.then(dve.scalar_tensor_tensor(o[:, :], o[:, :], pc[0][:, P_GG:P_GG + 1], ts[:, :], ALU.mult, ALU.mult))
                ch.then(dve.scalar_tensor_tensor(o[:, :], o[:, :], pc[0][:, P_GB:P_GB + 1], bon[:, :], ALU.add, ALU.add))
                dve.wait_ge(g_done, p + 1)
                dve.tensor_tensor(g[:, :], o[:, :], g[:, :], ALU.mult).then_inc(out_ready, 1)
                assert ch.n == LEN_END, ch.n

            def norm(p, more):
                if more:
                    projections(p + 1, p)
                else:
                    centre(p)
                    scale_norm(p)

            LEN_PAIR, LEN_END, LEN_PREP, LEN_F, LEN_B = 18, 2, 9, 5, 4
            pair_loop(dve, projections, both, norm)


def merge_stage(nc, hbm, merged):
    with Stage(nc, "mg") as st:
        w = [st.sb(f"w{j}", 128, D) for j in range(2)]
        branch = [st.sb("oR", 128, KT, T), st.sb("oA", 128, KT, T)]
        gate = [st.sb(f"gate{j}", 128, T) for j in range(2)]
        ps = st.psum()

        def two(name):
            return st.sems(f"{name}0 {name}1")

        w_ready, in_ready, logit_ready, gate_done, proj_ready, proj_done = (two(n) for n in (
            "w_ready", "in_ready", "logit_ready", "gate_done", "proj_ready", "proj_done"))
        added, = st.sems("added")
        block = st.block()

        @block.sync
        def _(sp):
            for j in range(2):
                sp.dma_start(w[j][:, :], hbm["w_merge"][j]).then_inc(w_ready[j], 16)
                for k in range(KT):
                    sp.dma_start(branch[j][:, k, :], hbm[("o_rw", "o_att")[j]][:, k, :]).then_inc(in_ready[j], 16)
                sp.dma_start(gate[j][:, :], hbm["logits"][j]).then_inc(logit_ready[j], 16)
            with sp.Fori(1, KT, 1) as i:
                for j in range(2):
                    sp.wait_ge(proj_ready[j], i)
                    sp.dma_start(w[j][:, :], hbm["w_merge"][bass.ds(i * 2 + j, 1), :, :].rearrange("a p n -> (a p) n")).then_inc(w_ready[j], 16)
                    sp.wait_ge((proj_done[0], added)[j], i + (1 - j))
                    sp.dma_start(gate[j][:, :], hbm["logits"][bass.ds(i * 2 + j, 1), :, :].rearrange("a p n -> (a p) n")).then_inc(logit_ready[j], 16)
            for j in range(2):
                sp.wait_ge(logit_ready[j], 16 * KT)

        @block.tensor
        def _(pe):
            for j in range(2):
                pe.sem_inc(proj_done[j], 1)
            with pe.Fori(0, KT, 1) as i:
                for j in range(2):
                    pe.wait_ge(w_ready[j], i * 16 + 16)
                    pe.wait_ge(in_ready[j], 16 * KT)
                    pe.wait_ge(proj_done[j], i + 1)
                    dense_block(pe, ps, 3 * j, w[j], branch[j]).then_inc(proj_ready[j], 1)

        @block.scalar
        def _(act):
            with act.Fori(0, KT, 1) as i:
                for j in range(2):
                    act.wait_ge(logit_ready[j], i * 16 + 16)
                    act.activation(gate[j][:, :], gate[j][:, :], ACT.Sigmoid).then_inc(gate_done[j], 1)

        @block.vector
        def _(dve):
            with dve.Fori(0, KT, 1) as i:
                out = merged[:, bass.ds(i, 1), :].rearrange("p a t -> p (a t)")
                for j in range(2):
                    dve.wait_ge(gate_done[j], i + 1)
                    dve.wait_ge(proj_ready[j], i + 1)
                    dve.tensor_tensor(gate[1][:, :] if j else out, set_of(ps, 3 * j), gate[j][:, :], ALU.mult).then_inc(proj_done[j], 1)
                for j in range(2):
                    dve.wait_ge(proj_done[j], i + 2)
                dve.tensor_tensor(out, out, gate[1][:, :], ALU.add).then_inc(added, 1)
                dve.wait_ge(added, i + 1)


def out_stage(nc, hbm, xT, merged):
    with Stage(nc, "ou") as st:
        w = [st.sb(f"w{i}", 128, D) for i in range(2)]
        ps = st.psum()
        w_ready = st.sems("w0 w1")
        z_ready, z_done = st.sems("z_ready z_done")
        block = st.block()

        @block.sync
        def _(sp):
            for s in range(2):
                sp.dma_start(w[s][:, :], hbm["w_out"][s]).then_inc(w_ready[s], 16)
            with sp.Fori(1, KT // 2, 1) as i:
                for s in range(2):
                    sp.wait_ge(z_ready, i * 2 + (s - 1))
                    sp.dma_start(w[s][:, :], hbm["w_out"][bass.ds(i * 2 + s, 1), :, :].rearrange("a p n -> (a p) n")).then_inc(w_ready[s], 16)

        @block.tensor
        def _(pe):
            pe.sem_inc(z_done, 2)
            with pe.Fori(0, KT // 2, 1) as i:
                for s in range(2):
                    pe.wait_ge(w_ready[s], i * 16 + 16)
                    pe.wait_ge(z_done, i * 2 + (s + 1))
                    dense_block(pe, ps, 3 * s, w[s], merged).then_inc(z_ready, 1)

        @block.vector
        def _(dve):
            with dve.Fori(0, KT // 2, 1) as i:
                for s in range(2):
                    x = xT[:, bass.ds(i * 2 + s, 1), :].rearrange("p a t -> p (a t)")
                    dve.wait_ge(z_ready, i * 2 + s + 1)
                    dve.scalar_tensor_tensor(x, x, ALPHA, set_of(ps, 3 * s), ALU.mult, ALU.add).then_inc(z_done, 1)


def ff_stage(nc, hbm, xT, acc):
    with Stage(nc, "ff") as st:
        w = [st.sb(f"w{i}", 128, D) for i in range(2)]
        hid = st.sb("hid", 128, KT, T)
        ps = st.psum()
        w_ready = st.sems("w0 w1")
        init_done, z_ready, h_relu, h_done, a_done, passed = st.sems("init_done z_ready h_relu h_done a_done passed")
        block = st.block()

        @block.sync
        def _(sp):
            for s in range(2):
                sp.dma_start(w[s][:, :], hbm["w_ff"][s]).then_inc(w_ready[s], 16)
            with sp.Fori(1, FFG * 8, 1) as i:
                for s in range(2):
                    sp.wait_ge(z_ready, i * 2 + (s - 1))
                    sp.dma_start(w[s][:, :], hbm["w_ff"][bass.ds(i * 2 + s, 1), :, :].rearrange("a p n -> (a p) n")).then_inc(w_ready[s], 16)

        @block.tensor
        def _(pe):
            pe.sem_inc(h_done, 2)
            pe.sem_inc(a_done, 2)
            with pe.Fori(0, FFG, 1) as f:
                with pe.Fori(0, KT // 2, 1) as i:
                    for s in range(2):
                        pe.wait_ge(w_ready[s], f * 128 + i * 16 + 16)
                        pe.wait_ge(h_done, f * 8 + i * 2 + (s + 1))
                        pe.wait_ge(a_done, f * 8 + (s + 1))
                        dense_block(pe, ps, 3 * s, w[s], xT).then_inc(z_ready, 1)
                with pe.Fori(0, KT // 2, 1) as i:
                    for s in range(2):
                        pe.wait_ge(w_ready[s], f * 128 + i * 16 + 80)
                        pe.wait_ge(h_done, f * 8 + 10)
                        pe.wait_ge(a_done, f * 8 + i * 2 + (s + 1))
                        dense_block(pe, ps, 3 * s, w[s], hid).then_inc(z_ready, 1)

        @block.scalar
        def _(act):
            with act.Fori(0, FFG, 1) as f:
                with act.Fori(0, KT // 2, 1) as i:
                    for s in range(2):
                        x = hid[:, bass.ds(i * 2 + s, 1), :].rearrange("p a t -> p (a t)")
                        act.wait_ge(z_ready, f * 16 + i * 2 + s + 1)
                        act.activation(x, set_of(ps, 3 * s), ACT.Relu).then_inc(h_relu, 1)
                        act.wait_ge(h_relu, f * 8 + i * 2 + s + 1)
                        settle(act, passed)
                        act.activation(x, x, ACT.Square).then_inc(h_done, 1)

        @block.vector
        def _(dve):
            dve.tensor_scalar(acc[:, :, :], xT[:, :, :], ALPHA, None, ALU.mult).then_inc(init_done, 1)
            dve.wait_ge(init_done, 1)
            with dve.Fori(0, FFG, 1) as f:
                with dve.Fori(0, KT // 2, 1) as i:
                    for s in range(2):
                        x = acc[:, bass.ds(i * 2 + s, 1), :].rearrange("p a t -> p (a t)")
                        dve.wait_ge(z_ready, f * 16 + i * 2 + s + 9)
                        dve.wait_ge(a_done, f * 8 + 2)
                        dve.tensor_tensor(x, x, set_of(ps, 3 * s), ALU.add).then_inc(a_done, 1)


def norm_stage(nc, hbm, tag, cst, glob, y, gcol, bcol, store):
    with Stage(nc, tag) as st:
        sq = [st.sb(f"sq{i}", 128, T) for i in range(2)]
        mean, rstd = st.sb("mean", 128, T), st.sb("rstd", 128, T)
        ps = st.psum()
        (m_ready, m_done, centred_d, centred_p, sq_done, sq_used, v_ready, s_done, r_done, scaled_d, scaled_p, y_done,
         stored) = st.sems("m_ready m_done centred_d centred_p sq_done sq_used v_ready s_done r_done scaled_d scaled_p y_done stored")
        ones = cst[:, C_ONES:C_ONES + 128]
        H = 768
        block = st.block()

        @block.tensor
        def _(pe):
            for j, (t0, n) in enumerate(SPANS):
                for k in range(KT):
                    last = pe.matmul(ps[:, j, 0:n], ones, y[:, k, t0:t0 + n], start=(k == 0), stop=(k == KT - 1))
            last.then_inc(m_ready, 1)
            for k in range(KT):
                pe.wait_ge(sq_done, k + 1)
                for j, (t0, n) in enumerate(SPANS):
                    last = pe.matmul(ps[:, 3 + j, 0:n], ones, sq[k % 2][:, t0:t0 + n], start=(k == 0), stop=(k == KT - 1))
                last.then_inc(sq_used, 1)

        @block.scalar
        def _(act):
            act.wait_ge(m_ready, 1)
            act.activation(mean[:, :], set_of(ps, 0), ACT.Copy, scale=1.0 / D).then_inc(m_done, 1)
            for k in range(KT):
                act.wait_ge(centred_d, k + 1)
                act.wait_ge(centred_p, k + 1)
                if k >= 2:
                    act.wait_ge(sq_used, k - 1)
                act.activation(sq[k % 2][:, :], y[:, k, :], ACT.Square).then_inc(sq_done, 1)
            act.wait_ge(sq_used, KT)
            act.activation(rstd[:, :], set_of(ps, 3), ACT.Ln, bias=cst[:, C_EPS + 2:C_EPS + 3], scale=1.0 / D).then_inc(s_done, 1)
            act.wait_ge(s_done, 1)
            act.activation(rstd[:, :], rstd[:, :], ACT.Exp, scale=-0.5).then_inc(r_done, 1)
            for k in range(KT):
                act.wait_ge(scaled_d, k + 1)
                act.wait_ge(scaled_p, k + 1)
                act.activation(y[:, k, :], y[:, k, :], ACT.Identity, bias=glob[:, bcol + k:bcol + k + 1],
                               scale=glob[:, gcol + k:gcol + k + 1]).then_inc(y_done, 1)

        def halves(eng, t0, t1, centred, scaled):
            eng.wait_ge(m_done, 1)
            for k in range(KT):
                eng.tensor_tensor(y[:, k, t0:t1], y[:, k, t0:t1], mean[:, t0:t1], ALU.subtract).then_inc(centred, 1)
            eng.wait_ge(r_done, 1)
            eng.wait_ge(sq_done, KT)
            eng.wait_ge(centred, KT)
            for k in range(KT):
                eng.tensor_tensor(y[:, k, t0:t1], y[:, k, t0:t1], rstd[:, t0:t1], ALU.mult).then_inc(scaled, 1)

        @block.vector
        def _(dve):
            halves(dve, 0, H, centred_d, scaled_d)

        @block.gpsimd
        def _(pool):
            halves(pool, H, T, centred_p, scaled_p)

        if store:
            @block.sync
            def _(sp):
                for k in range(KT):
                    sp.wait_ge(y_done, k + 1)
                    sp.dma_start(hbm["y"][128 * k:128 * k + 128, :], y[:, k, :]).then_inc(stored, 16)
                sp.wait_ge(stored, 16 * KT)


def encoder_layer(nc, hbm):
    hbm["o_att"] = nc.dram_tensor("o_att", [128, KT, T], F32).ap()
    hbm["o_rw"] = nc.dram_tensor("o_rw", [128, KT, T], F32).ap()
    hbm["logits"] = nc.dram_tensor("logits", [2 * KT, 128, T], F32).ap()
    with ExitStack() as ctx:
        def sb(name, *shape):
            return ctx.enter_context(nc.sbuf_tensor(name, list(shape), F32))

        xT = sb("xT", 128, KT, T)
        cst = sb("cst", 128, NCONST)
        glob = sb("glob", 128, NGLOB + 3)
        load_stage(nc, hbm, xT, cst, glob)
        with ExitStack() as a:
            def sa(name, *shape):
                return a.enter_context(nc.sbuf_tensor(name, list(shape), F32))

            qs, qp = sa("qs", 128, QH * SEQ_S), sa("qp", 128, QH * SEQ_P)
            ks, kp = sa("ks", 128, KVH * SEQ_S), sa("kp", 128, KVH * SEQ_P)
            vt = sa("vt", 128, T // 128, KVH * HD)
            attention_heads(nc, hbm, xT, cst, glob, qs, qp, ks, kp, vt)
            attention_core(nc, hbm, cst, qs, qp, ks, kp, vt)
        with ExitStack() as a:
            low = [a.enter_context(nc.sbuf_tensor(f"low{i}", [128, T], F32)) for i in range(3)]
            low_rank_stage(nc, hbm, xT, glob, low)
            rwkv_stage(nc, hbm, xT, cst, low)
        with ExitStack() as a:
            merged = a.enter_context(nc.sbuf_tensor("merged", [128, KT, T], F32))
            merge_stage(nc, hbm, merged)
            out_stage(nc, hbm, xT, merged)
        norm_stage(nc, hbm, "n1", cst, glob, xT, G_L1G, G_L1B, False)
        acc = sb("acc", 128, KT, T)
        ff_stage(nc, hbm, xT, acc)
        norm_stage(nc, hbm, "n2", cst, glob, acc, G_L2G, G_L2B, True)


def constants():
    import numpy as np
    c = np.zeros((128, NCONST), np.float32)
    p = np.arange(128)
    c[:, C_ID:C_ID + 128] = np.eye(128)
    for i in range(128):
        if (i // 32) % 2 == 0:
            c[i + 32, C_PERM + i] = -1.0
        else:
            c[i - 32, C_PERM + i] = 1.0
    c[:, C_ONES:C_ONES + 128] = 1.0
    c[:, C_BONES:C_BONES + 128] = p[:, None] // 64 == p[None, :] // 64
    s, t = (p % CH)[:, None], np.arange(CH)[None, :]
    for d in range(2):
        strict, incl = (t > s, t >= s) if d == 0 else (t < s, t <= s)
        at = C_MAB + 128 * d
        c[:, at:at + 64], c[:, at + 64:at + 128] = strict, -incl.astype(np.float32)
        at = C_MAK + 128 * d
        c[:, at:at + 64], c[:, at + 64:at + 128] = strict, incl
        i, j = (p % 32)[:, None], np.arange(32)[None, :]
        for l in range(5):
            b = 1 << l
            m = (i // (2 * b) == j // (2 * b)) & (i // b > j // b if d == 0 else i // b < j // b)
            if l == 0:
                m = (i // 2 == j // 2) & (i < j if d == 0 else i > j)
            c[:, C_LVL + 160 * d + 32 * l:C_LVL + 160 * d + 32 * l + 32] = -m.astype(np.float32)
    c[:, C_ID32:C_ID32 + 32] = (p % 32)[:, None] == np.arange(32)[None, :]
    for j in range(2):
        c[:, C_BLK + 32 * j:C_BLK + 32 * j + 32] = ((p // 32) % 2 == j)[:, None]
        c[:, C_SEL + j] = (p // 32) % 2 == j
    c[:, C_FLAG:C_FLAG + 2 * STEPS] = 1.0
    for at in (0, STEPS - 1, STEPS, STEPS + 1):
        c[:, C_FLAG + at] = 0.0
    c[:, C_EPS], c[:, C_EPS + 1], c[:, C_EPS + 2] = RMS_EPS, GN_EPS, LN_EPS
    c[:, C_ID64:C_ID64 + 64] = (p % 64)[:, None] == np.arange(64)[None, :]
    return c


def rope_tables():
    import numpy as np
    out = []
    for n in (SEQ_S, SEQ_P):
        tok = np.arange(n)
        half = HD // 2
        inv = (np.float32(10000.0) ** (-np.arange(0, half, 2, dtype=np.float32) / np.float32(half))).astype(np.float32)
        f = np.arange(HD)
        pos = np.where((f // 64 == 0)[:, None], (tok // 64)[None, :], (tok % 64)[None, :]).astype(np.float32)
        out.append(pos * inv[f % 32][:, None])
    ang = np.concatenate(out, axis=1).astype(np.float32)
    return np.cos(ang), np.sin(ang)


def lay_out(inp):
    import numpy as np

    def blocks(w):
        k, n = w.shape
        return w.reshape(k // 128, 128, n // 128, 128).transpose(2, 1, 0, 3).reshape(n // 128, 128, k)

    def cols(v):
        return v.reshape(-1, 128).T

    g = {k: np.asarray(v)[0] for k, v in inp.items() if not k.startswith("x_")}
    a = {}
    a["xT"] = np.concatenate([np.asarray(inp["x_sample"])[0].T, np.asarray(inp["x_prompt"])[0].T], axis=1)
    a["w_in"] = blocks(g["w_in"])
    gates = a["w_in"][B_GATE:]
    pr, pa = blocks(g["w_proj_rwkv"]), blocks(g["w_proj_attn"])
    a["w_gate"] = np.stack([gates[:KT], gates[KT:]], axis=1).reshape(2 * KT, 128, D)
    a["w_merge"] = np.stack([pr, pa], axis=1).reshape(2 * KT, 128, D)
    a["w_in"] = a["w_in"][:B_GATE]
    a["w_out"] = blocks(g["w_out"])
    f1 = blocks(g["w_ff1"]).reshape(FFG, 8, 128, D)
    f2 = np.stack([blocks(g["w_ff2"][1024 * f:1024 * f + 1024]) for f in range(FFG)])
    a["w_ff"] = np.concatenate([f1, f2], axis=1).reshape(16 * FFG, 128, D)
    up = [g["rw_w_up"].reshape(128, D), g["rw_a_up"].reshape(128, D), g["rw_g_up"]]
    a["w_low"] = np.stack([u.reshape(128, PAIRS, 128) for u in up], axis=2).transpose(1, 0, 2, 3).reshape(PAIRS, 128, 384)
    mp, mn = cols(g["rw_mu_prev"]), cols(g["rw_mu_next"])
    low0 = 3 * PAIRS
    a["glob"] = np.concatenate([mp[:, low0:], mn[:, low0:], cols(g["q_norm"]), cols(g["k_norm"]), np.zeros((128, 8), np.float32)] +
                               [cols(g[n]) for n in ("ln1_g", "ln1_b", "ln2_g", "ln2_b")], axis=1)
    per = [mp[:, c * PAIRS:(c + 1) * PAIRS] for c in range(3)] + [mn[:, c * PAIRS:(c + 1) * PAIRS] for c in range(3)]
    per += [cols(g["rw_w0"][d]) for d in range(2)] + [cols(g["rw_a0"][d]) for d in range(2)]
    per += [cols(g[n]) for n in ("rw_k_k", "rw_k_a", "rw_r_k", "rw_gn_g", "rw_gn_b")]
    a["pcols"] = np.stack(per, axis=2).transpose(1, 0, 2)
    a["consts"] = constants()
    a["cos"], a["sin"] = rope_tables()
    return {k: np.ascontiguousarray(v) for k, v in a.items()}


def kernel(**inputs):
    import numpy as np
    import concourse.bacc as bacc
    from concourse.bass_utils import run_bass_kernel_spmd

    nc = bacc.Bacc("TRN2", target_bir_lowering=False, num_devices=1)
    arrays = lay_out(inputs)
    hbm = {name: nc.dram_tensor(f"in_{name}", a.shape, mybir.dt.from_np(a.dtype), kind="ExternalInput").ap()
           for name, a in arrays.items()}
    hbm["y"] = nc.dram_tensor("out_y", (D, T), F32, kind="ExternalOutput").ap()
    encoder_layer(nc, hbm)
    r = run_bass_kernel_spmd(nc, [{f"in_{name}": a for name, a in arrays.items()}], core_ids=[0])
    y = r.results[0]["out_y"]
    return (np.ascontiguousarray(y[:, SEQ_S:].T)[None], np.ascontiguousarray(y[:, :SEQ_S].T)[None])
```
